# Optimizing a Trainium2 kernel written in Bass

```python
import jax, jax.numpy as jnp
from jax import lax
import numpy as np

D_MODEL = 2048
BATCH = 1
SEQ = 256
DEPTH = 1

N_ATTN_HEADS = 8
HEAD_DIM = 128
ATTN_WIDTH = N_ATTN_HEADS * HEAD_DIM
POOL_WIDTH = D_MODEL - ATTN_WIDTH
POOL_WINDOWS = (2, 4, 8, 16)
N_POOL_GROUPS = len(POOL_WINDOWS)
POOL_GROUP_DIM = POOL_WIDTH // N_POOL_GROUPS
MIX_WIDTH = ATTN_WIDTH + POOL_WIDTH
IN_PROJ_WIDTH = 3 * ATTN_WIDTH + POOL_WIDTH
MOBA_BLOCK = 256
MOBA_TOPK = 3
Q_CHUNK = 32
ROT_DIM = HEAD_DIM // 4
ROPE_THETA = 500000.0
D_FF = 5632
EPS = 1e-6
NEG_INF = -1e30
MAX_POS_OFFSET = 1024

kernel_name = "hymba_moba_pool_macaron_layer"

def rmsnorm(x, gain):
    xf = x.astype(jnp.float32)
    inv = lax.rsqrt(jnp.mean(xf * xf, axis=-1, keepdims=True) + EPS)
    return (xf * inv * gain.astype(jnp.float32)).astype(x.dtype)

def swiglu(h, w_gate, w_up, w_down):
    return (jax.nn.silu(h @ w_gate) * (h @ w_up)) @ w_down

def partial_rope(x, positions):
    inv_freq = ROPE_THETA ** (-jnp.arange(0, ROT_DIM, 2, dtype=jnp.float32) / ROT_DIM)
    ang = positions.astype(jnp.float32)[:, None, :, None] * inv_freq
    cos, sin = jnp.cos(ang), jnp.sin(ang)
    xr = x[..., :ROT_DIM].astype(jnp.float32)
    x1, x2 = xr[..., :ROT_DIM // 2], xr[..., ROT_DIM // 2:]
    rot = jnp.concatenate([x1 * cos - x2 * sin, x2 * cos + x1 * sin], axis=-1).astype(x.dtype)
    return jnp.concatenate([rot, x[..., ROT_DIM:]], axis=-1)

def moba_attention(q, k, v):
    B, H, S, Dh = q.shape
    nb = -(-S // MOBA_BLOCK)
    s_pad = nb * MOBA_BLOCK
    pad = ((0, 0), (0, 0), (0, s_pad - S), (0, 0))
    kb = jnp.pad(k, pad).reshape(B, H, nb, MOBA_BLOCK, Dh)
    vb = jnp.pad(v, pad).reshape(B, H, nb, MOBA_BLOCK, Dh)
    k_mean = jnp.mean(kb.astype(jnp.float32), axis=3)
    topk = min(MOBA_TOPK, nb)
    scale = HEAD_DIM ** -0.5
    n_chunks = S // Q_CHUNK
    q_chunks = q.reshape(B, H, n_chunks, Q_CHUNK, Dh).transpose(2, 0, 1, 3, 4)
    b_idx = jnp.arange(B)[:, None, None, None]
    h_idx = jnp.arange(H)[None, :, None, None]
    block_ids = jnp.arange(nb)

    def chunk_attn(args):
        c, qc = args
        q_start = c * Q_CHUNK
        qblk = q_start // MOBA_BLOCK
        gate = jnp.einsum('bhqd,bhnd->bhqn', qc.astype(jnp.float32), k_mean)
        gate = jnp.where(block_ids < qblk, gate, NEG_INF)
        _, sel = lax.top_k(gate, topk)
        sel_valid = sel < qblk
        k_sel = kb[b_idx, h_idx, sel]
        v_sel = vb[b_idx, h_idx, sel]
        s_sel = jnp.einsum('bhqd,bhqjpd->bhqjp', qc, k_sel).astype(jnp.float32) * scale
        s_sel = jnp.where(sel_valid[..., None], s_sel, NEG_INF).reshape(B, H, Q_CHUNK, topk * MOBA_BLOCK)
        k_own = lax.dynamic_index_in_dim(kb, qblk, axis=2, keepdims=False)
        v_own = lax.dynamic_index_in_dim(vb, qblk, axis=2, keepdims=False)
        s_own = jnp.einsum('bhqd,bhpd->bhqp', qc, k_own).astype(jnp.float32) * scale
        q_pos = q_start + jnp.arange(Q_CHUNK)
        k_pos = qblk * MOBA_BLOCK + jnp.arange(MOBA_BLOCK)
        s_own = jnp.where(k_pos[None, :] <= q_pos[:, None], s_own, NEG_INF)
        p = jax.nn.softmax(jnp.concatenate([s_sel, s_own], axis=-1), axis=-1)
        p_sel = p[..., :topk * MOBA_BLOCK].reshape(B, H, Q_CHUNK, topk, MOBA_BLOCK).astype(v.dtype)
        p_own = p[..., topk * MOBA_BLOCK:].astype(v.dtype)
        return (jnp.einsum('bhqjp,bhqjpd->bhqd', p_sel, v_sel)
                + jnp.einsum('bhqp,bhpd->bhqd', p_own, v_own))

    out = lax.map(chunk_attn, (jnp.arange(n_chunks), q_chunks))
    return out.transpose(1, 2, 0, 3, 4).reshape(B, H, S, Dh)

def multiscale_pool(u, pool_w, pool_scale):
    B, S, _ = u.shape
    ug = u.reshape(B, S, N_POOL_GROUPS, POOL_GROUP_DIM).astype(jnp.float32)
    csum = jnp.pad(jnp.cumsum(ug, axis=1), ((0, 0), (1, 0), (0, 0), (0, 0)))
    t = jnp.arange(S)
    windows = jnp.array(POOL_WINDOWS, dtype=jnp.int32)
    start = jnp.maximum(t[:, None] + 1 - windows[None, :], 0)
    count = (t[:, None] + 1 - start).astype(jnp.float32)
    g_idx = jnp.arange(N_POOL_GROUPS)[None, :]
    window_sum = csum[:, 1:] - csum[:, start, g_idx]
    pooled = (window_sum / count[None, :, :, None] - ug).astype(u.dtype)
    y = jnp.einsum('bsgc,gcd->bsgd', pooled, pool_w).reshape(B, S, POOL_WIDTH)
    return y * pool_scale

def setup_inputs(seed: int = 0) -> dict:
    key = jax.random.key(seed)
    ks = jax.random.split(key, 20)
    f32 = jnp.float32

    def normal(k, shape, fan_in):
        return jax.random.normal(k, shape, f32) * (fan_in ** -0.5)

    def gain(k, shape):
        return 1.0 + 0.02 * jax.random.normal(k, shape, f32)

    x = jax.random.normal(ks[0], (BATCH, SEQ, D_MODEL), f32)
    offsets = jax.random.randint(ks[1], (BATCH, 1), 0, MAX_POS_OFFSET, dtype=jnp.int32)
    positions = (jnp.arange(SEQ, dtype=jnp.int32)[None, :] + offsets).astype(jnp.int32)
    return {
        "x": x,
        "positions": positions,
        "norm_ffn1": gain(ks[2], (DEPTH, D_MODEL)),
        "w1_gate": normal(ks[3], (DEPTH, D_MODEL, D_FF), D_MODEL),
        "w1_up": normal(ks[4], (DEPTH, D_MODEL, D_FF), D_MODEL),
        "w1_down": normal(ks[5], (DEPTH, D_FF, D_MODEL), D_FF),
        "norm_mix": gain(ks[6], (DEPTH, D_MODEL)),
        "w_in": normal(ks[7], (DEPTH, D_MODEL, IN_PROJ_WIDTH), D_MODEL),
        "pool_w": normal(ks[8], (DEPTH, N_POOL_GROUPS, POOL_GROUP_DIM, POOL_GROUP_DIM), POOL_GROUP_DIM),
        "pool_scale": 1.0 + 0.1 * jax.random.normal(ks[9], (DEPTH, POOL_WIDTH), f32),
        "w_out": normal(ks[10], (DEPTH, MIX_WIDTH, D_MODEL), MIX_WIDTH),
        "norm_ffn2": gain(ks[11], (DEPTH, D_MODEL)),
        "w2_gate": normal(ks[12], (DEPTH, D_MODEL, D_FF), D_MODEL),
        "w2_up": normal(ks[13], (DEPTH, D_MODEL, D_FF), D_MODEL),
        "w2_down": normal(ks[14], (DEPTH, D_FF, D_MODEL), D_FF),
        "norm_final": gain(ks[15], (D_MODEL,)),
    }

def reference(x, positions, norm_ffn1, w1_gate, w1_up, w1_down, norm_mix, w_in, pool_w,
              pool_scale, w_out, norm_ffn2, w2_gate, w2_up, w2_down, norm_final):
    B, S, _ = x.shape
    for l in range(DEPTH):
        x = x + 0.5 * swiglu(rmsnorm(x, norm_ffn1[l]), w1_gate[l], w1_up[l], w1_down[l])
        h = rmsnorm(x, norm_mix[l])
        proj = h @ w_in[l]
        q, k, v, u = jnp.split(proj, [ATTN_WIDTH, 2 * ATTN_WIDTH, 3 * ATTN_WIDTH], axis=-1)
        to_heads = lambda t: t.reshape(B, S, N_ATTN_HEADS, HEAD_DIM).transpose(0, 2, 1, 3)
        q = partial_rope(to_heads(q), positions)
        k = partial_rope(to_heads(k), positions)
        attn = moba_attention(q, k, to_heads(v))
        attn = attn.transpose(0, 2, 1, 3).reshape(B, S, ATTN_WIDTH)
        pooled = multiscale_pool(u, pool_w[l], pool_scale[l])
        x = x + jnp.concatenate([attn, pooled], axis=-1) @ w_out[l]
        x = x + 0.5 * swiglu(rmsnorm(x, norm_ffn2[l]), w2_gate[l], w2_up[l], w2_down[l])
    return rmsnorm(x, norm_final)


_drawn_inputs = setup_inputs


def setup_inputs(seed=0):
    import zlib

    import numpy as np

    out = dict(_drawn_inputs(seed))
    spreads = {}
    factors = {'norm_ffn1': 6.471, 'norm_mix': 5.027, 'norm_ffn2': 8.0, 'norm_final': 2.747}
    for name, (base, spread) in spreads.items():
        noise = np.random.default_rng([zlib.crc32(name.encode()), seed]).standard_normal(out[name].shape)
        drawn = base * np.exp(spread * noise) if base else spread * noise
        out[name] = __import__('jax').numpy.asarray(drawn.astype(out[name].dtype))
    for name, factor in factors.items():
        out[name] = (out[name] * factor).astype(out[name].dtype)
    return out
```

```python
from contextlib import ExitStack

import numpy as np

import concourse.bass as bass
from concourse import mybir

F32 = mybir.dt.float32
F32R = mybir.dt.float32r
I32 = mybir.dt.int32
ALU = mybir.AluOpType
ACT = mybir.ActivationFunctionType
AX_X = mybir.AxisListType.X

P = 128
D = 2048
S = 256
FF = 5632
HEADS = 8
HD = 128
AW = HEADS * HD
WINDOWS = (2, 4, 8, 16)
GROUPS = len(WINDOWS)
ROT = HD // 4
THETA = 500000.0
EPS = 1e-6
MASKED = -1e30
SCALE = HD ** -0.5

KT = D // P
FT = FF // P
SB = 4
QCOLS = SB * P
GATE_SBS = FF // QCOLS
PIECE_K = 2
SB_PIECES = KT // PIECE_K
DOWN_PAIRS = KT // 2
DOWN_COLS = 2 * P
DOWN_CHUNKS = [(11 * a + b, n) for a in range(4) for b, n in ((0, 6), (6, 5))]
DOWN_PIECES = [(11 * a + b, n) for a in range(4) for b, n in ((0, 3), (3, 3), (6, 3), (9, 2))]
PAIR_PIECES = len(DOWN_PIECES)
RAW_SLOTS = 4
SPLIT_SLOTS = 4
TURN = 2 * RAW_SLOTS
PIECE = PIECE_K * QCOLS

FFN_TURNS = (2 * GATE_SBS * SB_PIECES + DOWN_PAIRS * PAIR_PIECES) // TURN
GATE_TURNS = 2 * GATE_SBS * SB_PIECES // TURN
MID_TURNS = 12

Q0, K0, Q1, K1, V0, V1, U0, U1, W0 = range(0, 72, 8)
MID_PIECES = MID_TURNS * TURN
HEAD_STEP = 3
SCORES_AT, TURN_AT, VALUES_AT = 36, 39, 43
POOL_HI_AT, POOL_LO_AT = 67, 68
W0_ORDER = (0, 1, 3, 2)

TWO_PI = 2 * np.pi
PI_A = 6.28125
PI_B = float(np.float32(np.round((TWO_PI - PI_A) * 2.0 ** 20) / 2.0 ** 20))
PI_C = float(np.float32(TWO_PI - PI_A - PI_B))
ROUND_MAGIC = 1.5 * 2.0 ** 23
PI_32 = float(np.nextafter(np.float32(np.pi), np.float32(0)))


def layer_kernel(nc, x, positions, norm_ffn1, w1_gate, w1_up, w1_down, norm_mix, w_in, pool_w,
                 pool_scale, w_out, norm_ffn2, w2_gate, w2_up, w2_down, norm_final,
                 c_ident, c_mask, c_ratio, c_freq, out):
    with ExitStack() as ctx:
        place = [(nc.sbuf_base + 31) // 32 * 32]

        def at(name, shape, dt, offset=None):
            size = 4
            for n in shape[1:]:
                size *= n
            if offset is None:
                offset = place[0]
                place[0] += (size + 31) // 32 * 32
            return nc.alloc_sbuf_tensor_at(name, shape, dt, offset=offset)

        xT = at("xT", [P, KT, S], F32)
        act_at = place[0]
        act = at("act", [P, KT, 2 * S], F32R)
        act32 = at("act32", [P, KT, 2 * S], F32, act_at)
        h_at = place[0]
        h = at("h", [P, FT, 2 * S], F32R)
        h32 = at("h32", [P, FT, 2 * S], F32, h_at)
        raw = at("raw", [P, RAW_SLOTS, 2 * PIECE], F32)
        w_hi = at("w_hi", [P, SPLIT_SLOTS, PIECE], F32R)
        w_lo = at("w_lo", [P, SPLIT_SLOTS, PIECE], F32R)
        squares = at("squares", [P, 2 * S], F32)
        square_sum = at("square_sum", [P, 2 * S], F32)
        r_row = at("r_row", [P, S], F32)
        ones = at("ones", [P, P], F32)
        ident = at("ident", [P, P], F32)
        gains = at("gains", [P, 4 * KT + 8], F32)
        r_col = at("r_col", [P, 2], F32)
        col_tmp = at("col_tmp", [P, 2, 2], F32)
        assert place[0] <= nc.sbuf_usable_end
        rows = at("rows", [P, 2, D], F32, h_at)
        end = place[0]
        place[0] = h_at + KT * 2 * S * 4
        qk = at("qk", [P, 2 * HEADS, S], F32)
        v = at("v", [P, 2, AW], F32)
        u = at("u", [P, 2 * GROUPS, S], F32)
        pool_at = place[0]
        window = at("window", [P, 2, 2, S], F32)
        rope_tmp = at("rope_tmp", [ROT, 4, S], F32, pool_at)
        pool_w_sb = at("pool_w_sb", [P, GROUPS, 2, 2 * P], F32)
        mask = at("mask", [P, 2, S], F32)
        cos = at("cos", [ROT, S], F32)
        sin = at("sin", [ROT, S], F32)
        ratio = at("ratio", [P, GROUPS, 16], F32)
        probs_at = place[0]
        probs = at("probs", [P, 2, 2 * S], F32)
        trig = at("trig", [ROT, 4, S], F32, probs_at)
        pos = at("pos", [ROT, S], I32)
        probsT = at("probsT", [P, 2, 3 * P], F32, place[0] - (S * 4))
        place[0] += 3 * P * 2 * 4 - S * 4
        negmax = at("negmax", [P, 2, 2], F32)
        rowsum = at("rowsum", [P, 2, 2], F32)
        rowinv = at("rowinv", [P, 2, 2], F32)
        freq = at("freq", [ROT, 2], F32)
        assert place[0] <= h_at + FT * 2 * S * 4, place[0] - h_at
        place[0] = end
        gain_rows = at("gain_rows", [4 * KT + 8, P], F32, h_at + 16384)

        banks = ctx.enter_context(nc.psum_tensor("banks", [P, 8, 512], F32))

        def sem(name):
            return ctx.enter_context(nc.semaphore(name))

        const_landed = sem("const_landed")
        x_landed = [sem(f"x_landed{j}") for j in range(4)]
        mixconst_landed = sem("mixconst_landed")
        raw_landed = [sem(f"raw_landed{j}") for j in range(RAW_SLOTS)]
        hi_ready = sem("hi_ready")
        lo_ready = sem("lo_ready")
        piece_used = sem("piece_used")
        ones_ready = sem("ones_ready")
        gains_turned = sem("gains_turned")
        gains_ready = sem("gains_ready")
        x_turned = sem("x_turned")
        quad_read = sem("quad_read")
        x_updated = sem("x_updated")
        act_hi_ready = sem("act_hi_ready")
        act_ready = sem("act_ready")
        half_copied = sem("half_copied")
        gate_scaled = sem("gate_scaled")
        silu_ready = sem("silu_ready")
        up_scaled = sem("up_scaled")
        product_ready = sem("product_ready")
        h_hi_ready = sem("h_hi_ready")
        h_ready = sem("h_ready")
        squares_ready = sem("squares_ready")
        squares_taken = sem("squares_taken")
        sumsq_ready = sem("sumsq_ready")
        meansq_ready = sem("meansq_ready")
        roots_ready = sem("roots_ready")
        newton_step = sem("newton_step")
        r_ready = sem("r_ready")
        trig_step = sem("trig_step")
        sines_ready = sem("sines_ready")
        trig_ready = sem("trig_ready")
        qk_scaled = sem("qk_scaled")
        rope_shuffled = sem("rope_shuffled")
        rope_scaled = sem("rope_scaled")
        qk_ready = sem("qk_ready")
        v_ready = sem("v_ready")
        u_ready = sem("u_ready")
        window_step = sem("window_step")
        pool_step = sem("pool_step")
        pooled_hi_groups = sem("pooled_hi_groups")
        pooled_lo_groups = sem("pooled_lo_groups")
        pool_mixed = sem("pool_mixed")
        pool_mix_hi = sem("pool_mix_hi")
        pool_mix_ready = sem("pool_mix_ready")
        scores_ready = sem("scores_ready")
        scores_masked = sem("scores_masked")
        negmax_ready = sem("negmax_ready")
        exp_ready = sem("exp_ready")
        rowinv_ready = sem("rowinv_ready")
        probs_ready = sem("probs_ready")
        probs_turned = sem("probs_turned")
        probsT_ready = sem("probsT_ready")
        values_ready = sem("values_ready")
        attn_hi_ready = sem("attn_hi_ready")
        attn_ready = sem("attn_ready")
        final_turned = sem("final_turned")
        row_scaled_act = sem("row_scaled_act")
        row_scaled_dve = sem("row_scaled_dve")
        out_stored = sem("out_stored")

        ffns = [
            dict(gate=w1_gate, up=w1_up, down=w1_down, turn=0, sb=0, upd=4, act=0),
            dict(gate=w2_gate, up=w2_up, down=w2_down, turn=FFN_TURNS + MID_TURNS,
                 sb=2 * GATE_SBS + DOWN_PAIRS + 10, upd=4 + DOWN_PAIRS + 4, act=2 * KT),
        ]
        MID_TURN = FFN_TURNS
        MID_SB = 2 * GATE_SBS + DOWN_PAIRS
        MID_UPD = 4 + DOWN_PAIRS
        END_TURN = 2 * FFN_TURNS + MID_TURNS
        FINAL_UPD = 4 + 2 * DOWN_PAIRS + 4
        gain_of = lambda norm, k: gains[:, norm * KT + k:norm * KT + k + 1]

        block = ctx.enter_context(nc.Block())

        @block.sync
        def _(sp):
            def load(dst, src, turn, c, wait=True):
                if wait:
                    sp.wait_ge(lo_ready, turn * TURN + 2 * c - 2 * RAW_SLOTS + 2)
                sp.dma_start(dst, src).then_inc(raw_landed[c % RAW_SLOTS], 16)

            def load_wide(w, kc, col, turn, c, wait=True):
                load(raw[:, c % RAW_SLOTS, :].rearrange("p (t n) -> p t n", n=QCOLS),
                     w[kc * 4 * P:(kc + 1) * 4 * P, bass.ds(col, QCOLS)]
                     .rearrange("(t p) n -> p t n", p=P), turn, c, wait)

            def load_gate_up(f, i, first):
                turn = f["turn"] + 2 * i
                for c in range(8):
                    load_wide(f["gate"] if c < 4 else f["up"], c % 4, i * QCOLS, turn, c,
                              not (first and c < RAW_SLOTS))

            def load_down_two(f, i):
                turn = f["turn"] + GATE_TURNS + 4 * i
                for c in range(16):
                    k, n = DOWN_CHUNKS[c % 8]
                    load(raw[:, c % RAW_SLOTS, 0:n * DOWN_COLS]
                         .rearrange("p (t n) -> p t n", n=DOWN_COLS),
                         f["down"][k * P:(k + n) * P,
                                   bass.ds(i * 2 * DOWN_COLS + (c // 8) * DOWN_COLS, DOWN_COLS)]
                         .rearrange("(t p) n -> p t n", p=P), turn, c)

            for f in ffns:
                load_gate_up(f, 0, f["turn"] == 0)
                with sp.Fori(1, GATE_SBS) as i:
                    load_gate_up(f, i, False)
                with sp.Fori(0, DOWN_PAIRS // 2) as i:
                    load_down_two(f, i)
                if f["turn"] == 0:
                    for c in range(4 * MID_TURNS):
                        sb, kc = c // 4, c % 4
                        if c < 32:
                            col = (0, AW, QCOLS, AW + QCOLS, 2 * AW, 2 * AW + QCOLS,
                                   3 * AW + QCOLS, 3 * AW)[sb]
                            load_wide(w_in, kc, col, MID_TURN, c)
                        else:
                            load_wide(w_out, W0_ORDER[kc], (sb - 8) * QCOLS, MID_TURN, c)
            for j in range(4):
                sp.wait_ge(row_scaled_act, j + 1)
                sp.wait_ge(row_scaled_dve, j + 1)
                sp.dma_start(out[:, j * 512:(j + 1) * 512].rearrange("(t p) n -> p t n", p=P),
                             rows[:, :, j * 512:(j + 1) * 512]).then_inc(out_stored, 16)
            sp.wait_ge(out_stored, 4 * 16)

        @block.tensor
        def _(pe):
            def multiply(turn, p, bank, tiles, k_first, width, operand, last_tile):
                s = p % SPLIT_SLOTS
                pe.wait_ge(lo_ready, turn * TURN + p + 1)
                for b in range(width // P):
                    for j, k in enumerate(tiles):
                        w = slice(j * width + b * P, j * width + (b + 1) * P)
                        first, last = k == k_first, k == last_tile
                        pe.matmul(banks[:, bank + b, :], w_hi[:, s, w], operand[:, k, :],
                                  start=first, stop=last, skip_group_check=True)
                        mm = pe.matmul(banks[:, bank + b, 0:S], w_lo[:, s, w],
                                       operand[:, k, 0:S], start=False, stop=last,
                                       skip_group_check=True)
                mm.then_inc(piece_used, 1)

            def multiply_sb(turn, p, quad, operand=None, act_from=None):
                n = p % SB_PIECES
                if act_from is not None:
                    pe.wait_ge(act_ready, act_from + PIECE_K * (n + 1))
                multiply(turn, p, 4 * quad, (PIECE_K * n, PIECE_K * n + 1), 0, QCOLS,
                         act if operand is None else operand, KT - 1)

            def sum_squares(norm, cols):
                pe.wait_ge(squares_taken, 8 * (norm + 1))
                pe.wait_ge(ones_ready, 1)
                b = 4
                if norm < 3:
                    for half in range(2):
                        mm = pe.matmul(banks[:, b, 0:S], ones[:, :],
                                       square_sum[:, half * S:(half + 1) * S],
                                       start=half == 0, stop=half == 1)
                if cols:
                    for t in range(2):
                        for half in range(2):
                            mm = pe.matmul(banks[:, b, S + t:S + t + 1],
                                           square_sum[:, half * S + t * P:half * S + (t + 1) * P],
                                           ones[:, 0:1], start=half == 0, stop=half == 1)
                mm.then_inc(sumsq_ready, 1)

            def gate_up(f, i, first):
                turn, m = f["turn"] + 2 * i, f["sb"] + 2 * i
                if f["turn"] or not first:
                    pe.wait_ge(quad_read, m - 1)
                for p in range(8):
                    multiply_sb(turn, p, 0, act_from=f["act"] if first else None)
                if first:
                    if f["turn"]:
                        pe.wait_ge(quad_read, m)
                    sum_squares(0 if f["turn"] == 0 else 2, False)
                    pe.wait_ge(meansq_ready, 1 if f["turn"] == 0 else 3)
                else:
                    pe.wait_ge(quad_read, m)
                for p in range(8, 16):
                    multiply_sb(turn, p, 1)

            def down_two(f, i):
                turn, m = f["turn"] + GATE_TURNS + 4 * i, f["sb"] + 2 * GATE_SBS + 2 * i
                hs = 0 if f["turn"] == 0 else GATE_SBS
                for p in range(2 * PAIR_PIECES):
                    quad = p // PAIR_PIECES
                    if p % PAIR_PIECES == 0:
                        pe.wait_ge(quad_read, m + quad - 1)
                    k, n = DOWN_PIECES[p % PAIR_PIECES]
                    if quad == 0:
                        pe.wait_ge(h_ready, hs + (k + n - 1) // SB + 1)
                    multiply(turn, p, 4 * quad, range(k, k + n), 0, DOWN_COLS, h, FT - 1)

            def multiply_rows(p, vb):
                n, s = p % SB_PIECES, p % SPLIT_SLOTS
                pe.wait_ge(lo_ready, MID_TURN * TURN + p + 1)
                for t in range(2):
                    bank = banks[:, 2 - 2 * vb + t, :]
                    hi, lo = slice(t * P, (t + 1) * P), slice(S + t * P, S + (t + 1) * P)
                    for j in range(PIECE_K):
                        k = PIECE_K * n + j
                        w = slice(j * QCOLS, (j + 1) * QCOLS)
                        pe.matmul(bank, act[:, k, hi], w_hi[:, s, w], start=k == 0, stop=False)
                        pe.matmul(bank, act[:, k, lo], w_hi[:, s, w], start=False, stop=False)
                        mm = pe.matmul(bank, act[:, k, hi], w_lo[:, s, w], start=False,
                                       stop=k == KT - 1)
                mm.then_inc(piece_used, 1)

            def head_scores(hd):
                if hd == 0:
                    pe.wait_ge(quad_read, MID_SB + 4)
                pe.wait_ge(qk_ready, 2 if hd < 4 else 4)
                if hd >= 2:
                    pe.wait_ge(scores_masked, hd - 1)
                for t in range(2):
                    mm = pe.matmul(banks[:, 4 + hd % 2, t * S:(t + 1) * S],
                                   qk[:, hd, t * P:(t + 1) * P], qk[:, HEADS + hd, :],
                                   start=True, stop=True)
                mm.then_inc(scores_ready, 1)

            def head_turn(hd):
                pe.wait_ge(probs_ready, hd + 1)
                if hd >= 1:
                    pe.wait_ge(probsT_ready, hd)
                for j, (q, k) in enumerate(((0, 0), (1, 0), (1, 1))):
                    mm = pe.transpose(banks[:, 6, j * P:(j + 1) * P],
                                      probs[:, hd % 2, q * S + k * P:q * S + (k + 1) * P],
                                      ident[:, :])
                mm.then_inc(probs_turned, 1)

            def head_values(hd):
                pe.wait_ge(probsT_ready, hd + 1)
                pe.wait_ge(v_ready, 2 if hd < 4 else 4)
                if hd >= 1:
                    pe.wait_ge(attn_ready, hd)
                d = slice(hd * HD, (hd + 1) * HD)
                pe.matmul(banks[:, 7, 0:S], v[:, 0, d], probsT[:, hd % 2, 0:S],
                          start=True, stop=False, skip_group_check=True)
                pe.matmul(banks[:, 7, P:S], v[:, 1, d], probsT[:, hd % 2, S:S + P],
                          start=False, stop=True, skip_group_check=True).then_inc(values_ready, 1)

            def mix_groups(gs, done, n):
                pe.wait_ge(done, n)
                pe.wait_ge(attn_ready, HEADS)
                if gs[0] == 0:
                    pe.wait_ge(pool_mix_ready, 4)
                for g in gs:
                    for db in range(2):
                        for c in range(2):
                            mm = pe.matmul(banks[:, 4 + 2 * (g % 2) + db, 0:S],
                                           pool_w_sb[:, g, c, db * P:(db + 1) * P],
                                           u[:, 2 * g + c, :], start=c == 0, stop=c == 1)
                        mm.then_inc(pool_mixed, 1)

            def middle():
                for p in range(MID_PIECES):
                    if p < V0:
                        if p % 8 == 0:
                            pe.wait_ge(quad_read, MID_SB - 1 + p // 8)
                        if p == K0:
                            pe.wait_ge(meansq_ready, 2)
                        multiply_sb(MID_TURN, p, (p // 8) % 2, act_from=KT if p < 8 else None)
                        if p == K0 - 1:
                            pe.wait_ge(quad_read, MID_SB)
                            sum_squares(1, True)
                    elif p < U0:
                        if p == V0:
                            pe.wait_ge(quad_read, MID_SB + 3)
                        multiply_rows(p, (p - V0) // 8)
                    elif p < W0:
                        if p == U0:
                            pe.wait_ge(v_ready, 4)
                        if p == U1:
                            pe.wait_ge(quad_read, MID_SB + 5)
                        multiply_sb(MID_TURN, p, 0)
                    else:
                        sb, n = (p - W0) // 8, p % 8
                        if n == 0:
                            pe.wait_ge(quad_read, MID_SB + 6 if sb == 0 else MID_SB + 5 + sb)
                        k = 4 * W0_ORDER[n // 2] + PIECE_K * (n % 2)
                        if sb == 0:
                            if k < 8:
                                pe.wait_ge(attn_ready, k + 2)
                            else:
                                pe.wait_ge(pool_mix_ready, (k - 12 if k >= 12 else k - 4) + 2)
                        multiply(MID_TURN, p, 4 * (sb % 2), (k, k + 1), 0, QCOLS, h, 11)
                    if (p - SCORES_AT) % HEAD_STEP == 0 and 0 <= (p - SCORES_AT) // HEAD_STEP < HEADS:
                        head_scores((p - SCORES_AT) // HEAD_STEP)
                    if (p - TURN_AT) % HEAD_STEP == 0 and 0 <= (p - TURN_AT) // HEAD_STEP < HEADS:
                        head_turn((p - TURN_AT) // HEAD_STEP)
                    if (p - VALUES_AT) % HEAD_STEP == 0 and 0 <= (p - VALUES_AT) // HEAD_STEP < HEADS:
                        head_values((p - VALUES_AT) // HEAD_STEP)
                    if p == POOL_HI_AT:
                        mix_groups((2, 3), pooled_hi_groups, 2)
                    if p == POOL_LO_AT:
                        mix_groups((0, 1), pooled_lo_groups, 2)

            pe.wait_ge(const_landed, 16 * 6)
            pe.transpose(banks[:, 7, 0:4 * KT + 8], gain_rows[:, :],
                         ident[0:4 * KT + 8, 0:4 * KT + 8]).then_inc(gains_turned, 1)
            pe.wait_ge(gains_ready, 1)
            for j in range(4):
                pe.wait_ge(x_landed[j], 16)
                for k in range(4 * j, 4 * j + 4):
                    for t in range(2):
                        mm = pe.transpose(banks[:, k // 2, (k % 2) * S + t * P:(k % 2) * S + (t + 1) * P],
                                          rows[:, t, k * P:(k + 1) * P], ident[:, :])
                mm.then_inc(x_turned, 1)
            pe.wait_ge(x_updated, 4)
            for f in ffns:
                gate_up(f, 0, True)
                with pe.Fori(1, GATE_SBS) as i:
                    gate_up(f, i, False)
                with pe.Fori(0, DOWN_PAIRS // 2) as i:
                    down_two(f, i)
                if f["turn"] == 0:
                    middle()
            pe.wait_ge(quad_read, ffns[1]["sb"] + 2 * GATE_SBS + DOWN_PAIRS)
            sum_squares(3, True)
            for j in range(4):
                pe.wait_ge(act_hi_ready, 3 * KT + 4 * j + 4)
                if j == 0:
                    pe.wait_ge(meansq_ready, 4)
                for t in range(2):
                    for k in range(4):
                        mm = pe.transpose(banks[:, 4 * t + j, k * P:(k + 1) * P],
                                          act32[:, 4 * j + k, t * P:(t + 1) * P], ident[:, :])
                mm.then_inc(final_turned, 1)

        @block.scalar
        def _(act_e):
            def round_piece(turn, p, n, width, fresh=False):
                s = p % SPLIT_SLOTS
                if p % 2 == 0:
                    act_e.wait_ge(raw_landed[(p // 2) % RAW_SLOTS], (turn + p // TURN + 1) * 16)
                if not (fresh and p < SPLIT_SLOTS):
                    act_e.wait_ge(piece_used, turn * TURN + p - SPLIT_SLOTS + 1)
                off, n = piece_span(p, n, width)
                act_e.activation(w_hi[:, s, 0:n], raw[:, (p // 2) % RAW_SLOTS, off:off + n],
                                 ACT.Copy).then_inc(hi_ready, 1)

            def copy_half(quad, tiles, dst, count):
                act_e.wait_ge(piece_used, count)
                act_e.activation(dst, banks[:, 4 * quad:4 * quad + tiles, S:2 * S],
                                 ACT.Copy).then_inc(half_copied, 1)

            def feed(norm, k, n, upd):
                act_e.wait_ge(x_updated, upd)
                for j in range(n):
                    if norm < 3:
                        act_e.activation(act[:, bass.ds(k + j, 1), 0:S], xT[:, bass.ds(k + j, 1), :],
                                         ACT.Copy, scale=gains[:, bass.ds(k + norm * KT + j, 1)])\
                             .then_inc(act_hi_ready, 1)
                    else:
                        act_e.activation(act32[:, bass.ds(k + j, 1), 0:S], xT[:, bass.ds(k + j, 1), :],
                                         ACT.Copy, scale=gains[:, bass.ds(k + norm * KT + j, 1)])\
                             .then_inc(act_hi_ready, 1)

            def square(k, done=None):
                if done is not None:
                    act_e.wait_ge(squares_taken, done)
                act_e.activation(squares[:, :].rearrange("p (a q) -> p a q", a=2),
                                 xT[:, bass.ds(k, 2), :], ACT.Square).then_inc(squares_ready, 1)

            def square_roots(norm):
                act_e.wait_ge(meansq_ready, norm + 1)
                if norm in COL_NORMS:
                    ins = act_e.activation(col_tmp[:, 0, :], r_col[:, :], ACT.Sqrt)
                if norm in ROW_NORMS:
                    ins = act_e.activation(squares[:, 0:S], r_row[:, :], ACT.Sqrt)
                ins.then_inc(roots_ready, 1)

            def gate_up(f, i, first):
                turn, m = f["turn"] + 2 * i, f["sb"] + 2 * i
                fi = (0 if f["turn"] == 0 else GATE_SBS) + i
                fresh = first and f["turn"] == 0
                for p in range(16):
                    if p == 14:
                        act_e.wait_ge(gate_scaled, fi + 1)
                    round_piece(turn, p, PIECE_K, QCOLS, fresh)
                    if fresh and p < 8 and p % 2 == 1:
                        j = p // 2
                        feed(0, 4 * j, 4, j + 1)
                        square(4 * j, 2 * j if j else None)
                        square(4 * j + 2, 2 * j + 1)
                    if first and f["turn"] and p in (3, 5):
                        w_update(3, p)
                    if not first and p == 3:
                        copy_half(1, SB, h32[:, bass.ds(SB * i - SB, SB), S:2 * S], turn * TURN)
                    if not first and p == 5:
                        round_h(SB * i - SB, fi)
                    if p == 11:
                        copy_half(0, SB, h32[:, bass.ds(SB * i, SB), 0:S], (turn + 1) * TURN)
                    if first and p == 11:
                        square_roots(0 if fresh else 2)
                    if p == 14:
                        silu(SB * i)

            def silu(k):
                act_e.activation(h32[:, bass.ds(k, SB), 0:S], h32[:, bass.ds(k, SB), 0:S],
                                 ACT.Silu).then_inc(silu_ready, 1)

            def round_h(k, n):
                act_e.wait_ge(product_ready, n)
                act_e.activation(h[:, bass.ds(k, SB), 0:S], h32[:, bass.ds(k, SB), S:2 * S],
                                 ACT.Copy).then_inc(h_hi_ready, 1)

            def pair_update(f, k, pair, count, step):
                norm = 1 if f["turn"] == 0 else 3
                if step == 0:
                    act_e.wait_ge(piece_used, count)
                    quad = 1 if step_quad[0] else 0
                    act_e.activation(act32[:, bass.ds(k, 2), S:2 * S],
                                     banks[:, 4 * quad:4 * quad + 2, S:2 * S],
                                     ACT.Copy, scale=0.5).then_inc(half_copied, 1)
                else:
                    upd = f["upd"] + pair + 1
                    act_e.wait_ge(squares_taken, 8 * norm + pair)
                    feed(norm, k, 2, upd)
                    square(k)

            step_quad = [0]

            def down_two(f, i, first):
                turn = f["turn"] + GATE_TURNS + 4 * i
                for p in range(2 * PAIR_PIECES):
                    round_piece(turn, p, DOWN_PIECES[p % PAIR_PIECES][1], DOWN_COLS)
                    if first and p == 3:
                        copy_half(1, SB, h32[:, FT - SB:FT, S:2 * S], turn * TURN)
                    if first and p == 5:
                        round_h(FT - SB, (1 if f["turn"] == 0 else 2) * GATE_SBS)
                    if not first and p in (3, 5):
                        step_quad[0] = 1
                        pair_update(f, 4 * i - 2, 2 * i - 1, turn * TURN, p == 5)
                    if p in (19, 21):
                        step_quad[0] = 0
                        pair_update(f, 4 * i, 2 * i, turn * TURN + PAIR_PIECES, p == 21)

            def w_update(sb, p):
                k = SB * sb
                if p == 3:
                    act_e.wait_ge(piece_used, MID_TURN * TURN + W0 + 8 * (sb + 1))
                    act_e.activation(act32[:, k:k + SB, S:2 * S],
                                     banks[:, 4 * (sb % 2):4 * (sb % 2) + SB, S:2 * S],
                                     ACT.Copy).then_inc(half_copied, 1)
                else:
                    feed(2, k, SB, MID_UPD + sb + 1)
                    square(k, 16 + 2 * sb)
                    square(k + 2, 16 + 2 * sb + 1)

            def middle():
                for p in range(MID_PIECES):
                    round_piece(MID_TURN, p, PIECE_K, QCOLS)
                    if p == 3:
                        step_quad[0] = 1
                        pair_update(ffns[0], KT - 2, DOWN_PAIRS - 1, MID_TURN * TURN, 0)
                    if p == 4:
                        for dst, src in (
                            (pool_w_sb[:, :, :, :], pool_w.rearrange("g (c p) d -> p g c d", p=P)),
                            (mask[:, :, :], c_mask.rearrange("p (t k) -> p t k", t=2)),
                            (ratio[:, :, :], c_ratio.rearrange("p (g t) -> p g t", g=GROUPS)),
                            (freq[:, :], c_freq),
                            (pos[:, :], positions.broadcast_to((ROT, S))),
                        ):
                            act_e.dma_start(dst, src).then_inc(mixconst_landed, 16)
                    if p == 5:
                        pair_update(ffns[0], KT - 2, DOWN_PAIRS - 1, MID_TURN * TURN, 1)
                    if p == 11:
                        square_roots(1)
                    if p == 10:
                        act_e.wait_ge(trig_step, TRIG_STEPS)
                        act_e.activation(sin[:, :], trig[:, 1, :], ACT.Sin).then_inc(sines_ready, 1)
                        act_e.activation(cos[:, :], trig[:, 2, :], ACT.Sin).then_inc(sines_ready, 1)
                    if p >= 11 and p % 8 == 3 and p <= K1 + 11:
                        s = (p - 11) // 8
                        k = QK_TILES[s]
                        copy_half(s % 2, SB, qk[:, k:k + SB, :], MID_TURN * TURN + 8 * (s + 1))
                    if p in (V1 + 3, U0 + 3):
                        vb = (p - V1) // 8
                        act_e.wait_ge(piece_used, MID_TURN * TURN + V1 + 8 * vb)
                        act_e.wait_ge(r_ready, 2)
                        for t in range(2):
                            act_e.activation(v[:, t, vb * QCOLS:(vb + 1) * QCOLS],
                                             banks[:, 2 - 2 * vb + t, :], ACT.Copy,
                                             scale=r_col[:, t:t + 1]).then_inc(v_ready, 1)
                    if p in (U1 + 3, W0 + 3):
                        ub = (p - U1) // 8
                        copy_half(0, SB, u[:, SB - SB * ub:2 * SB - SB * ub, :],
                                  MID_TURN * TURN + U1 + 8 * ub)
                    hd = (p - SCORES_AT - 5) // HEAD_STEP
                    if (p - SCORES_AT - 5) % HEAD_STEP == 0 and 0 <= hd < HEADS:
                        act_e.wait_ge(negmax_ready, hd + 1)
                        for t in range(2):
                            row = probs[:, hd % 2, t * S:(t + 1) * S]
                            act_e.activation(row, row, ACT.Exp, bias=negmax[:, hd % 2, t:t + 1],
                                             accum_out=rowsum[:, hd % 2, t:t + 1])\
                                 .then_inc(exp_ready, 1)
                    hd = (p - TURN_AT - 4) // HEAD_STEP
                    if (p - TURN_AT - 4) % HEAD_STEP == 0 and 0 <= hd < HEADS:
                        act_e.wait_ge(probs_turned, hd + 1)
                        if hd >= 2:
                            act_e.wait_ge(values_ready, hd - 1)
                        act_e.activation(probsT[:, hd % 2, :], banks[:, 6, 0:3 * P],
                                         ACT.Copy).then_inc(probsT_ready, 1)
                    hd = (p - VALUES_AT - 4) // HEAD_STEP
                    if (p - VALUES_AT - 4) % HEAD_STEP == 0 and 0 <= hd < HEADS:
                        act_e.wait_ge(values_ready, hd + 1)
                        act_e.activation(h[:, hd, 0:S], banks[:, 7, 0:S],
                                         ACT.Copy).then_inc(attn_hi_ready, 1)
                    if p in (POOL_HI_AT + 4, POOL_LO_AT + 4):
                        gs = (2, 3) if p == POOL_HI_AT + 4 else (0, 1)
                        for j, g in enumerate(gs):
                            for db in range(2):
                                act_e.wait_ge(pool_mixed, (4 if gs[0] == 0 else 0) + 2 * j + db + 1)
                                act_e.activation(h[:, HEADS + 2 * g + db, 0:S],
                                                 banks[:, 4 + 2 * (g % 2) + db, 0:S], ACT.Copy,
                                                 scale=gains[:, 4 * KT + 2 * g + db:4 * KT + 2 * g + db + 1])\
                                     .then_inc(pool_mix_hi, 1)
                    if p >= W0 + 8 and p % 8 in (3, 5):
                        w_update((p - W0) // 8 - 1, p % 8)

            act_e.dma_start(ident[:, :], c_ident).then_inc(const_landed, 16)
            for n, g in enumerate((norm_ffn1, norm_mix, norm_ffn2)):
                act_e.dma_start(gain_rows[n * KT:(n + 1) * KT, :],
                                g.rearrange("l (k p) -> (l k) p", p=P)).then_inc(const_landed, 16)
            act_e.dma_start(gain_rows[3 * KT:4 * KT, :],
                            norm_final.rearrange("(k p) -> k p", p=P)).then_inc(const_landed, 16)
            act_e.dma_start(gain_rows[4 * KT:4 * KT + 8, :],
                            pool_scale.rearrange("l (k p) -> (l k) p", p=P)).then_inc(const_landed, 16)
            for j in range(4):
                act_e.dma_start(rows[:, :, j * 512:(j + 1) * 512],
                                x[:, j * 512:(j + 1) * 512].rearrange("(t p) n -> p t n", p=P))\
                     .then_inc(x_landed[j], 16)
            act_e.wait_ge(gains_ready, 1)
            for f in ffns:
                gate_up(f, 0, True)
                with act_e.Fori(1, GATE_SBS) as i:
                    gate_up(f, i, False)
                down_two(f, 0, True)
                with act_e.Fori(1, DOWN_PAIRS // 2) as i:
                    down_two(f, i, False)
                if f["turn"] == 0:
                    middle()
            step_quad[0] = 1
            for step in range(2):
                pair_update(ffns[1], KT - 2, DOWN_PAIRS - 1, END_TURN * TURN, step)
            square_roots(3)
            act_e.wait_ge(r_ready, 4)
            for j in range(4):
                act_e.wait_ge(final_turned, j + 1)
                act_e.activation(rows[:, 0, j * 512:(j + 1) * 512], banks[:, j, :], ACT.Copy,
                                 scale=r_col[:, 0:1]).then_inc(row_scaled_act, 1)

        @block.vector
        def _(dve):
            def split_piece(turn, p, n, width):
                s = p % SPLIT_SLOTS
                dve.wait_ge(hi_ready, turn * TURN + p + 1)
                off, n = piece_span(p, n, width)
                dve.tensor_tensor(w_lo[:, s, 0:n], raw[:, (p // 2) % RAW_SLOTS, off:off + n],
                                  w_hi[:, s, 0:n].bitcast(F32), ALU.subtract)\
                   .then_inc(lo_ready, 1)

            def feed(norm, k, n, count):
                for j in range(n):
                    dve.wait_ge(act_hi_ready, count + j + 1)
                    dve.scalar_tensor_tensor(
                        act[:, bass.ds(k + j, 1), S:2 * S], xT[:, bass.ds(k + j, 1), :],
                        gains[:, bass.ds(k + norm * KT + j, 1)],
                        act[:, bass.ds(k + j, 1), 0:S].bitcast(F32),
                        ALU.mult, ALU.subtract).then_inc(act_ready, 1)

            def mean_square(norm):
                dve.wait_ge(sumsq_ready, norm + 1)
                if norm in COL_NORMS:
                    ins = dve.tensor_scalar(r_col[:, :], banks[:, 4, S:S + 2], 1.0 / D, EPS,
                                            ALU.mult, ALU.add)
                if norm in ROW_NORMS:
                    ins = dve.tensor_scalar(r_row[:, :], banks[:, 4, 0:S], 1.0 / D, EPS,
                                            ALU.mult, ALU.add)
                ins.then_inc(meansq_ready, 1)

            newton_steps = [0]

            def inverse_root(norm):
                def step(ins):
                    newton_steps[0] += 1
                    ins.then_inc(newton_step, 1)
                    dve.wait_ge(newton_step, newton_steps[0])

                dve.wait_ge(roots_ready, norm + 1)
                todo = []
                if norm in COL_NORMS:
                    todo.append((r_col[:, :], col_tmp[:, 0, :], col_tmp[:, 1, :]))
                if norm in ROW_NORMS:
                    todo.append((r_row[:, :], squares[:, 0:S], squares[:, S:2 * S]))
                for ms, y, t in todo:
                    step(dve.reciprocal(y, y))
                    step(dve.tensor_tensor(t, y, y, ALU.mult))
                    step(dve.scalar_tensor_tensor(t, t, -0.5, ms, ALU.mult, ALU.mult))
                    ins = dve.scalar_tensor_tensor(ms, t, 1.5, y, ALU.add, ALU.mult)
                ins.then_inc(r_ready, 1)
                dve.wait_ge(r_ready, norm + 1)

            def across(row, n):
                return row.unsqueeze(1).to_broadcast([row.shape[0], n, S])

            def add_half(quad, dst, m, half):
                dve.wait_ge(half_copied, half)
                dve.tensor_tensor(dst, banks[:, 4 * quad:4 * quad + SB, 0:S], dst,
                                  ALU.add).then_inc(quad_read, 1)
                dve.wait_ge(quad_read, m)

            def gate_up(f, i, first):
                turn, m = f["turn"] + 2 * i, f["sb"] + 2 * i
                fi = (0 if f["turn"] == 0 else GATE_SBS) + i
                fresh = first and f["turn"] == 0
                norm = 0 if f["turn"] == 0 else 2
                for p in range(16):
                    split_piece(turn, p, PIECE_K, QCOLS)
                    if fresh and p in (1, 3, 5, 7):
                        feed(0, 4 * (p // 2), 4, 4 * (p // 2))
                    if first and f["turn"] and p in (3, 6):
                        w_update(3, p)
                    if not first and p == 3:
                        product(i, f, m)
                    if not first and p == 6:
                        split_h(SB * i - SB, fi)
                    if first and p == 10:
                        mean_square(norm)
                    if p == 11:
                        add_half(0, h32[:, bass.ds(SB * i, SB), 0:S], m + 1, m + 1)
                    if p == 12:
                        if first:
                            inverse_root(norm)
                        g = h32[:, bass.ds(SB * i, SB), 0:S]
                        dve.tensor_tensor(g, g, across(r_row[:, :], SB),
                                          ALU.mult).then_inc(gate_scaled, 1)

            def product(i, f, m):
                fi = (0 if f["turn"] == 0 else GATE_SBS) + i
                k = SB * i - SB
                up = h32[:, bass.ds(k, SB), S:2 * S]
                add_half(1, up, m, m)
                dve.tensor_tensor(up, up, across(r_row[:, :], SB), ALU.mult).then_inc(up_scaled, 1)
                dve.wait_ge(up_scaled, fi)
                dve.wait_ge(silu_ready, fi)
                dve.tensor_tensor(up, up, h32[:, bass.ds(k, SB), 0:S],
                                  ALU.mult).then_inc(product_ready, 1)

            def split_h(k, n):
                dve.wait_ge(h_hi_ready, n)
                dve.tensor_tensor(h[:, bass.ds(k, SB), S:2 * S], h32[:, bass.ds(k, SB), S:2 * S],
                                  h[:, bass.ds(k, SB), 0:S].bitcast(F32),
                                  ALU.subtract).then_inc(h_ready, 1)

            def update(quad, tiles, k, weight, m):
                dve.wait_ge(half_copied, m)
                xs = xT[:, bass.ds(k, tiles), :]
                dve.scalar_tensor_tensor(xs, banks[:, 4 * quad:4 * quad + tiles, 0:S], weight, xs,
                                         ALU.mult, ALU.add).then_inc(quad_read, 1)
                dve.wait_ge(quad_read, m)
                dve.tensor_tensor(xs, xs, act32[:, bass.ds(k, tiles), S:2 * S],
                                  ALU.add).then_inc(x_updated, 1)

            def pair_update(f, k, pair, quad, step):
                if step == 0:
                    update(quad, 2, k, 0.5, f["sb"] + 2 * GATE_SBS + pair + 1)
                elif f["turn"] == 0:
                    feed(1, k, 2, KT + k)

            def down_two(f, i, first):
                turn = f["turn"] + GATE_TURNS + 4 * i
                for p in range(2 * PAIR_PIECES):
                    split_piece(turn, p, DOWN_PIECES[p % PAIR_PIECES][1], DOWN_COLS)
                    if first and p == 3:
                        product(GATE_SBS, f, f["sb"] + 2 * GATE_SBS)
                    if first and p == 6:
                        split_h(FT - SB, (1 if f["turn"] == 0 else 2) * GATE_SBS)
                    if not first and p in (3, 6):
                        pair_update(f, 4 * i - 2, 2 * i - 1, 1, p == 6)
                    if p in (19, 22):
                        pair_update(f, 4 * i, 2 * i, 0, p == 22)

            def w_update(sb, p):
                if p == 3:
                    update(sb % 2, SB, SB * sb, 1.0, MID_SB + 6 + sb + 1)
                else:
                    feed(2, SB * sb, SB, 2 * KT + SB * sb)

            def angles():
                n = [0]
                ang, red, quarter, turns = (trig[:, j, :] for j in range(4))

                def step(ins):
                    n[0] += 1
                    ins.then_inc(trig_step, 1)
                    dve.wait_ge(trig_step, n[0])

                dve.wait_ge(mixconst_landed, 5 * 16)
                step(dve.tensor_copy(red, pos[:, :]))
                step(dve.tensor_scalar(ang, red, freq[:, 0:1], None, ALU.mult))
                step(dve.tensor_scalar(turns, ang, 1 / TWO_PI, ROUND_MAGIC, ALU.mult, ALU.add))
                step(dve.tensor_scalar(turns, turns, ROUND_MAGIC, None, ALU.subtract))
                step(dve.scalar_tensor_tensor(red, turns, -PI_A, ang, ALU.mult, ALU.add))
                step(dve.scalar_tensor_tensor(red, turns, -PI_B, red, ALU.mult, ALU.add))
                step(dve.scalar_tensor_tensor(red, turns, -PI_C, red, ALU.mult, ALU.add))
                step(dve.tensor_scalar(red, red, PI_32, -PI_32, ALU.min, ALU.max))
                step(dve.scalar_tensor_tensor(quarter, red, -1.0, red, ALU.mult, ALU.max))
                step(dve.tensor_scalar(quarter, quarter, -1.0, float(np.pi / 2), ALU.mult, ALU.add))
                assert n[0] == TRIG_STEPS

            def rotate(s, step):
                k = QK_TILES[s]
                heads = qk[:, k:k + SB, :]
                rot = qk[0:ROT, k:k + SB, :]
                if step == 0:
                    add_half(s % 2, heads, MID_SB + s + 1, MID_SB + s + 1)
                elif step == 1:
                    if s == 0:
                        inverse_root(1)
                    dve.tensor_tensor(heads, heads, across(r_row[:, :], SB),
                                      ALU.mult).then_inc(qk_scaled, 1)
                elif step == 2:
                    dve.wait_ge(qk_scaled, s + 1)
                    half = ROT // 2
                    dve.stream_shuffle(rope_tmp[:, :, :], rot,
                                       [(c + half) % ROT for c in range(ROT)])\
                       .then_inc(rope_shuffled, 1)
                elif step == 3:
                    dve.wait_ge(rope_shuffled, s + 1)
                    if s == 0:
                        dve.wait_ge(trig_ready, 1)
                    dve.tensor_tensor(rot, rot, across(cos[:, :], SB), ALU.mult)\
                       .then_inc(rope_scaled, 1)
                    dve.tensor_tensor(rope_tmp[:, :, :], rope_tmp[:, :, :], across(sin[:, :], SB),
                                      ALU.mult).then_inc(rope_scaled, 1)
                else:
                    dve.wait_ge(rope_scaled, 2 * s + 2)
                    dve.tensor_tensor(rot, rot, rope_tmp[:, :, :], ALU.add).then_inc(qk_ready, 1)

            def near_windows():
                n = [0]

                def step(ins):
                    n[0] += 1
                    ins.then_inc(window_step, 1)
                    dve.wait_ge(window_step, n[0])

                for g in (1, 0):
                    own = u[:, 2 * g:2 * g + 2, :]
                    cur = own
                    for j in range(g + 1):
                        d = 2 ** j
                        nxt = window[:, j % 2, :, :]
                        dve.tensor_copy(nxt[:, :, 0:d], cur[:, :, 0:d])
                        step(dve.tensor_tensor(nxt[:, :, d:S], cur[:, :, d:S], cur[:, :, 0:S - d],
                                               ALU.add))
                        cur = nxt
                    step(dve.tensor_tensor(cur[:, :, 0:16], cur[:, :, 0:16],
                                           ratio[:, g, :].unsqueeze(1).to_broadcast([P, 2, 16]),
                                           ALU.mult))
                    dve.scalar_tensor_tensor(own, cur, 1.0 / WINDOWS[g], own, ALU.mult,
                                             ALU.subtract).then_inc(pooled_lo_groups, 1)

            def middle():
                for p in range(MID_PIECES):
                    split_piece(MID_TURN, p, PIECE_K, QCOLS)
                    if p == 3:
                        pair_update(ffns[0], KT - 2, DOWN_PAIRS - 1, 1, 0)
                    if p == 6:
                        pair_update(ffns[0], KT - 2, DOWN_PAIRS - 1, 1, 1)
                    if p == 8:
                        angles()
                    if p == 10:
                        mean_square(1)
                    if p == 11:
                        dve.wait_ge(sines_ready, 2)
                        dve.tensor_scalar(sin[:, :], sin[:, :], freq[:, 1:2], None,
                                          ALU.mult).then_inc(trig_ready, 1)
                    if 11 <= p < K1 + 16 and 3 <= p % 8 <= 7:
                        rotate((p - 11) // 8, p % 8 - 3)
                    if p in (U1 + 3, W0 + 3):
                        ub = (p - U1) // 8
                        us = u[:, SB - SB * ub:2 * SB - SB * ub, :]
                        add_half(0, us, MID_SB + 5 + ub, MID_SB + 5 + ub)
                        dve.tensor_tensor(us, us, across(r_row[:, :], SB),
                                          ALU.mult).then_inc(u_ready, 1)
                        if ub == 1:
                            dve.wait_ge(u_ready, 2)
                            dve.wait_ge(pooled_hi_groups, 2)
                            near_windows()
                    hd = (p - SCORES_AT - 4) // HEAD_STEP
                    if (p - SCORES_AT - 4) % HEAD_STEP == 0 and 0 <= hd < HEADS:
                        if hd >= 2:
                            dve.wait_ge(probs_turned, hd - 1)
                        dve.wait_ge(scores_ready, hd + 1)
                        dve.scalar_tensor_tensor(
                            probs[:, hd % 2, :], banks[:, 4 + hd % 2, :], SCALE,
                            mask[:, :, :].rearrange("p t k -> p (t k)"),
                            ALU.mult, ALU.add).then_inc(scores_masked, 1)
                        dve.wait_ge(scores_masked, hd + 1)
                        dve.tensor_reduce(negmax[:, hd % 2, :],
                                          probs[:, hd % 2, :].rearrange("p (t k) -> p t k", t=2),
                                          AX_X, ALU.max, negate=True).then_inc(negmax_ready, 1)
                    hd = (p - SCORES_AT - 5) // HEAD_STEP
                    if (p - SCORES_AT - 5) % HEAD_STEP == 0 and 0 <= hd < HEADS:
                        dve.wait_ge(exp_ready, 2 * hd + 2)
                        dve.reciprocal(rowinv[:, hd % 2, :],
                                       rowsum[:, hd % 2, :]).then_inc(rowinv_ready, 1)
                        dve.wait_ge(rowinv_ready, hd + 1)
                        for t in range(2):
                            row = probs[:, hd % 2, t * S:(t + 1) * S]
                            ins = dve.tensor_scalar(row, row, rowinv[:, hd % 2, t:t + 1], None,
                                                    ALU.mult)
                        ins.then_inc(probs_ready, 1)
                    hd = (p - VALUES_AT - 5) // HEAD_STEP
                    if (p - VALUES_AT - 5) % HEAD_STEP == 0 and 0 <= hd < HEADS:
                        dve.wait_ge(attn_hi_ready, hd + 1)
                        dve.tensor_tensor(h[:, hd, S:2 * S], banks[:, 7, 0:S],
                                          h[:, hd, 0:S].bitcast(F32),
                                          ALU.subtract).then_inc(attn_ready, 1)
                    if p in (POOL_HI_AT + 4, POOL_LO_AT + 4):
                        gs = (2, 3) if p == POOL_HI_AT + 4 else (0, 1)
                        for j, g in enumerate(gs):
                            for db in range(2):
                                k = HEADS + 2 * g + db
                                dve.wait_ge(pool_mix_hi, (4 if gs[0] == 0 else 0) + 2 * j + db + 1)
                                dve.scalar_tensor_tensor(
                                    h[:, k, S:2 * S], banks[:, 4 + 2 * (g % 2) + db, 0:S],
                                    gains[:, 4 * KT + 2 * g + db:4 * KT + 2 * g + db + 1],
                                    h[:, k, 0:S].bitcast(F32), ALU.mult,
                                    ALU.subtract).then_inc(pool_mix_ready, 1)
                    if p >= W0 + 8 and p % 8 in (3, 6):
                        w_update((p - W0) // 8 - 1, p % 8)

            dve.memset(ones[:, :], 1.0).then_inc(ones_ready, 1)
            dve.wait_ge(gains_turned, 1)
            dve.tensor_copy(gains[:, :], banks[:, 7, 0:4 * KT + 8]).then_inc(gains_ready, 1)
            for j in range(4):
                dve.wait_ge(x_turned, j + 1)
                dve.tensor_copy(xT[:, 4 * j:4 * j + 4, :].rearrange("p (b k) q -> p b (k q)", b=2),
                                banks[:, 2 * j:2 * j + 2, :]).then_inc(x_updated, 1)
            for f in ffns:
                gate_up(f, 0, True)
                with dve.Fori(1, GATE_SBS) as i:
                    gate_up(f, i, False)
                down_two(f, 0, True)
                with dve.Fori(1, DOWN_PAIRS // 2) as i:
                    down_two(f, i, False)
                if f["turn"] == 0:
                    middle()
            pair_update(ffns[1], KT - 2, DOWN_PAIRS - 1, 1, 0)
            mean_square(3)
            inverse_root(3)
            for j in range(4):
                dve.wait_ge(final_turned, j + 1)
                dve.tensor_scalar(rows[:, 1, j * 512:(j + 1) * 512], banks[:, 4 + j, :],
                                  r_col[:, 1:2], None, ALU.mult).then_inc(row_scaled_dve, 1)

        @block.gpsimd
        def _(pool):
            def sum_squares(norm):
                for n in range(8):
                    pool.wait_ge(squares_ready, 8 * norm + n + 1)
                    if n == 0:
                        if norm:
                            pool.wait_ge(sumsq_ready, norm)
                        pool.tensor_copy(square_sum[:, :], squares[:, :]).then_inc(squares_taken, 1)
                    else:
                        pool.wait_ge(squares_taken, 8 * norm + n)
                        pool.tensor_tensor(square_sum[:, :], square_sum[:, :], squares[:, :],
                                           ALU.add).then_inc(squares_taken, 1)

            def far_windows():
                n = [0]

                def step(ins):
                    n[0] += 1
                    ins.then_inc(pool_step, 1)
                    pool.wait_ge(pool_step, n[0])

                for g in (3, 2):
                    own = u[:, 2 * g:2 * g + 2, :]
                    cur = own
                    for j in range(g + 1):
                        d = 2 ** j
                        nxt = window[:, j % 2, :, :]
                        pool.tensor_copy(nxt[:, :, 0:d], cur[:, :, 0:d])
                        step(pool.tensor_tensor(nxt[:, :, d:S], cur[:, :, d:S], cur[:, :, 0:S - d],
                                                ALU.add))
                        cur = nxt
                    step(pool.tensor_tensor(cur[:, :, 0:16], cur[:, :, 0:16],
                                            ratio[:, g, :].unsqueeze(1).to_broadcast([P, 2, 16]),
                                            ALU.mult))
                    step(pool.tensor_scalar(cur, cur, 1.0 / WINDOWS[g], None, ALU.mult))
                    pool.tensor_tensor(own, cur, own, ALU.subtract).then_inc(pooled_hi_groups, 1)

            for norm in range(4):
                sum_squares(norm)
                if norm == 1:
                    pool.wait_ge(qk_ready, 4)
                    pool.wait_ge(u_ready, 1)
                    far_windows()


TRIG_STEPS = 10
ROW_NORMS = (0, 1, 2)
COL_NORMS = (1, 3)
QK_TILES = (0, HEADS, SB, HEADS + SB)


def piece_span(p, n, width):
    first = (n if n * width == PIECE or n == 3 else 3) * width
    return (first if p % 2 else 0), n * width


_INS = ["x", "positions", "norm_ffn1", "w1_gate", "w1_up", "w1_down", "norm_mix", "w_in", "pool_w",
        "pool_scale", "w_out", "norm_ffn2", "w2_gate", "w2_up", "w2_down", "norm_final"]
_DROP_LEAD = {"x", "w1_gate", "w1_up", "w1_down", "w_in", "pool_w", "w_out", "w2_gate", "w2_up",
              "w2_down"}


def shape_constants():
    q = np.arange(P)[:, None]
    k = np.arange(S)[None, :]
    mask = np.concatenate([np.where(k <= q + t * P, 0.0, MASKED) for t in range(2)], axis=1)
    t = np.arange(16)
    ratio = np.concatenate([w / np.minimum(t + 1, w) for w in WINDOWS])
    freq = THETA ** (-np.arange(0, ROT, 2, dtype=np.float64) / ROT)
    sign = np.where(np.arange(ROT) < ROT // 2, -1.0, 1.0)
    f = np.float32
    return {
        "c_ident": np.eye(P, dtype=f),
        "c_mask": mask.astype(f),
        "c_ratio": np.broadcast_to(ratio.astype(f), (P, 16 * GROUPS)).copy(),
        "c_freq": np.stack([np.concatenate([freq, freq]), sign], axis=1).astype(f),
    }


def build(nc, args):
    layer_kernel(nc, **args)


def kernel(**inputs):
    import concourse.bacc as _bacc
    from concourse import mybir as _mybir
    from concourse.bass_utils import run_bass_kernel_spmd as _run

    nc = _bacc.Bacc("TRN2", target_bir_lowering=False, num_devices=1)
    arrays, args = {}, {}
    named = {n: np.ascontiguousarray(inputs[n]) for n in _INS}
    named.update(shape_constants())
    for name, a in named.items():
        arrays[f"in_{name}"] = a
        ap = nc.dram_tensor(f"in_{name}", a.shape, _mybir.dt.from_np(a.dtype),
                            kind="ExternalInput").ap()
        args[name] = ap[0] if name in _DROP_LEAD else ap
    o = nc.dram_tensor("out_0", (1, S, D), _mybir.dt.float32, kind="ExternalOutput").ap()
    args["out"] = o[0]
    build(nc, args)
    r = _run(nc, [arrays], core_ids=[0])
    return r.results[0]["out_0"]
```
